# Optimizing a Trainium2 kernel written in Bass

```python
import math, functools
import jax, jax.numpy as jnp
from jax import lax
import numpy as np

D_MODEL = 1024
BATCH = 1
SEQ = 512
DEPTH = 2
DEC_BATCH = 8
DEC_SEQ = 1
PAST_LEN = 4096
PAGE_SIZE = 128

N_MIXERS = 2
N_MLA_LAYERS = (DEPTH + 1) // 2
N_DIL_LAYERS = DEPTH // 2
MLA_HEADS = 16
MLA_NOPE = 64
MLA_ROPE = 32
MLA_VDIM = 64
MLA_Q_LORA = 384
MLA_KV_LORA = 256
ROPE_THETA = 10000.0
MLA_BLOCK_Q = 128
DIL_GROUPS = ((128, 1), (512, 4), (2048, 16))
DIL_HEADS = 8
DIL_HEAD_DIM = 64
D_FF = 4 * D_MODEL
EPS = 1e-6
NEG_INF = -1e30

kernel_name = "mla_dilated_swa_hybrid_step"

def rmsnorm(x, g):
    xf = x.astype(jnp.float32)
    y = xf * lax.rsqrt(jnp.mean(xf * xf, axis=-1, keepdims=True) + EPS)
    return (y * g.astype(jnp.float32)).astype(x.dtype)

def rope(x, pos):
    half = MLA_ROPE // 2
    inv = ROPE_THETA ** (-jnp.arange(half, dtype=jnp.float32) / half)
    ang = pos.astype(jnp.float32)[:, None] * inv[None, :]
    cos = jnp.cos(ang)[None, :, None, :]
    sin = jnp.sin(ang)[None, :, None, :]
    xf = x.astype(jnp.float32)
    x1, x2 = xf[..., :half], xf[..., half:]
    return jnp.concatenate([x1 * cos - x2 * sin, x1 * sin + x2 * cos], axis=-1).astype(x.dtype)

def sqrelu_ffn(h, w_up, w_down):
    return jnp.square(jax.nn.relu(h @ w_up)) @ w_down

def mla_project(x, pos, w_dq, g_q, w_uq, w_dkv, g_kv):
    B, T, _ = x.shape
    c_q = rmsnorm(x @ w_dq, g_q)
    q = (c_q @ w_uq).reshape(B, T, MLA_HEADS, MLA_NOPE + MLA_ROPE)
    q_nope = q[..., :MLA_NOPE]
    q_pe = rope(q[..., MLA_NOPE:], pos)
    kv_a = x @ w_dkv
    c_kv = rmsnorm(kv_a[..., :MLA_KV_LORA], g_kv)
    k_pe = rope(kv_a[..., None, MLA_KV_LORA:], pos)[:, :, 0]
    return q_nope, q_pe, c_kv, k_pe

def mla_prompt(x, w_dq, g_q, w_uq, w_dkv, g_kv, w_uk, w_uv, w_o):
    B, S, _ = x.shape
    pos = jnp.arange(S)
    q_nope, q_pe, c_kv, k_pe = mla_project(x, pos, w_dq, g_q, w_uq, w_dkv, g_kv)
    k_nope = jnp.einsum("bsc,chn->bshn", c_kv, w_uk)
    v = jnp.einsum("bsc,chv->bshv", c_kv, w_uv)
    nb = S // MLA_BLOCK_Q
    qn_b = jnp.moveaxis(q_nope.reshape(B, nb, MLA_BLOCK_Q, MLA_HEADS, MLA_NOPE), 1, 0)
    qp_b = jnp.moveaxis(q_pe.reshape(B, nb, MLA_BLOCK_Q, MLA_HEADS, MLA_ROPE), 1, 0)
    scale = (MLA_NOPE + MLA_ROPE) ** -0.5
    key_pos = jnp.arange(S)

    def block(args):
        qn, qp, q0 = args
        s = jnp.einsum("bqhn,bkhn->bhqk", qn, k_nope) + jnp.einsum("bqhr,bkr->bhqk", qp, k_pe)
        s = s.astype(jnp.float32) * scale
        qpos = q0 + jnp.arange(MLA_BLOCK_Q)
        s = jnp.where(key_pos[None, :] <= qpos[:, None], s, NEG_INF)
        p = jax.nn.softmax(s, axis=-1).astype(v.dtype)
        return jnp.einsum("bhqk,bkhv->bqhv", p, v)

    o = lax.map(block, (qn_b, qp_b, jnp.arange(nb) * MLA_BLOCK_Q))
    o = jnp.moveaxis(o, 0, 1).reshape(B, S, MLA_HEADS * MLA_VDIM)
    return o @ w_o, c_kv, k_pe

def mla_sample(x, ckv_pool, kpe_pool, page_table, w_dq, g_q, w_uq, w_dkv, g_kv, w_uk, w_uv, w_o):
    B, T, _ = x.shape
    past = page_table.shape[1] * PAGE_SIZE
    pos = past + jnp.arange(T)
    q_nope, q_pe, c_kv, k_pe = mla_project(x, pos, w_dq, g_q, w_uq, w_dkv, g_kv)
    ckv_past = ckv_pool[page_table].reshape(B, past, MLA_KV_LORA)
    kpe_past = kpe_pool[page_table].reshape(B, past, MLA_ROPE)
    q_lat = jnp.einsum("bthn,chn->bthc", q_nope, w_uk)
    scale = (MLA_NOPE + MLA_ROPE) ** -0.5
    s_past = jnp.einsum("bthc,bkc->bhtk", q_lat, ckv_past) + jnp.einsum("bthr,bkr->bhtk", q_pe, kpe_past)
    s_new = jnp.einsum("bthc,bkc->bhtk", q_lat, c_kv) + jnp.einsum("bthr,bkr->bhtk", q_pe, k_pe)
    causal = jnp.tril(jnp.ones((T, T), dtype=bool))
    s_new = jnp.where(causal, s_new.astype(jnp.float32), NEG_INF)
    s = jnp.concatenate([s_past.astype(jnp.float32), s_new], axis=-1) * scale
    p = jax.nn.softmax(s, axis=-1).astype(c_kv.dtype)
    o_lat = jnp.einsum("bhtk,bkc->bthc", p[..., :past], ckv_past) + jnp.einsum("bhtk,bkc->bthc", p[..., past:], c_kv)
    o = jnp.einsum("bthc,chv->bthv", o_lat, w_uv).reshape(B, T, MLA_HEADS * MLA_VDIM)
    return o @ w_o, c_kv, k_pe

def alibi_slopes():
    return jnp.power(2.0, -8.0 * jnp.arange(1, DIL_HEADS + 1, dtype=jnp.float32) / DIL_HEADS)

def _to_sub(a, d):
    B, S = a.shape[:2]
    rest = a.shape[2:]
    a = a.reshape((B, S // d, d) + rest)
    return jnp.moveaxis(a, 2, 1).reshape((B * d, S // d) + rest)

def _from_sub(a, B, d, L):
    a = a[:, :L]
    rest = a.shape[2:]
    a = jnp.moveaxis(a.reshape((B, d, L) + rest), 1, 2)
    return a.reshape((B, L * d) + rest)

def dilated_group_prompt(q, k, v, dilation, span, slopes):
    B, S, H, E = q.shape
    L = S // dilation
    nb = -(-L // span)
    pad = nb * span - L
    z = B * dilation
    qs, ks, vs = _to_sub(q, dilation), _to_sub(k, dilation), _to_sub(v, dilation)
    qb = jnp.pad(qs, ((0, 0), (0, pad), (0, 0), (0, 0))).reshape(z, nb, span, H, E)

    def band(a):
        ap = jnp.pad(a, ((0, 0), (span, pad), (0, 0), (0, 0))).reshape(z, nb + 1, span, H, E)
        return jnp.concatenate([ap[:, :-1], ap[:, 1:]], axis=2)

    kb, vb = band(ks), band(vs)
    qi = jnp.arange(span)[:, None]
    ki = jnp.arange(2 * span)[None, :]
    dist = qi + span - ki
    key_sub = (jnp.arange(nb) * span - span)[:, None, None] + ki[None]
    valid = (dist >= 0) & (dist <= span) & (key_sub >= 0)
    scale = DIL_HEAD_DIM ** -0.5
    s = jnp.einsum("znqhe,znkhe->znhqk", qb, kb).astype(jnp.float32) * scale
    s = s - slopes[:, None, None] * (dist * dilation).astype(jnp.float32)
    s = jnp.where(valid[None, :, None], s, NEG_INF)
    m = jnp.max(s, axis=-1)
    e = jnp.exp(s - m[..., None])
    den = jnp.sum(e, axis=-1)
    o = jnp.einsum("znhqk,znkhe->znqhe", e, vb.astype(jnp.float32)).reshape(z, nb * span, H, E)
    m = jnp.swapaxes(m, 2, 3).reshape(z, nb * span, H)
    den = jnp.swapaxes(den, 2, 3).reshape(z, nb * span, H)
    return _from_sub(o, B, dilation, L), _from_sub(m, B, dilation, L), _from_sub(den, B, dilation, L)

def dilated_group_sample(q, k, v, buf, window, dilation, span, slopes):
    B, T, H, E = q.shape
    WB = buf.shape[1]
    kv_all = jnp.concatenate([buf, jnp.stack([k, v], axis=2).astype(buf.dtype)], axis=1)
    idx = WB + jnp.arange(T)[:, None] - dilation * jnp.arange(span + 1)[None, :]
    valid = idx >= 0
    g = kv_all[:, jnp.maximum(idx, 0)]
    scale = DIL_HEAD_DIM ** -0.5
    s = jnp.einsum("bthe,btihe->bhti", q, g[:, :, :, 0]).astype(jnp.float32) * scale
    s = s - slopes[:, None, None] * (dilation * jnp.arange(span + 1)).astype(jnp.float32)
    s = jnp.where(valid[None, None], s, NEG_INF)
    m = jnp.max(s, axis=-1)
    e = jnp.exp(s - m[..., None])
    den = jnp.sum(e, axis=-1)
    o = jnp.einsum("bhti,btihe->bthe", e, g[:, :, :, 1].astype(jnp.float32))
    keep = min(window, WB + T)
    new_buf = kv_all[:, WB + T - keep:]
    return o, jnp.swapaxes(m, 1, 2), jnp.swapaxes(den, 1, 2), new_buf

def merge_groups(parts):
    M = functools.reduce(jnp.maximum, [m for _, m, _ in parts])
    num = sum(o * jnp.exp(m - M)[..., None] for o, m, _ in parts)
    den = sum(dn * jnp.exp(m - M) for _, m, dn in parts)
    return num / den[..., None]

def dil_prompt(x, w_qkv, w_o):
    B, S, _ = x.shape
    qkv = (x @ w_qkv).reshape(B, S, len(DIL_GROUPS), 3, DIL_HEADS, DIL_HEAD_DIM)
    slopes = alibi_slopes()
    parts, bufs = [], []
    for gi, (window, dilation) in enumerate(DIL_GROUPS):
        q, k, v = qkv[:, :, gi, 0], qkv[:, :, gi, 1], qkv[:, :, gi, 2]
        parts.append(dilated_group_prompt(q, k, v, dilation, window // dilation, slopes))
        bufs.append(jnp.stack([k, v], axis=2)[:, S - min(window, S):])
    o = merge_groups(parts).astype(x.dtype).reshape(B, S, DIL_HEADS * DIL_HEAD_DIM)
    return o @ w_o, bufs

def dil_sample(x, bufs_in, w_qkv, w_o):
    B, T, _ = x.shape
    qkv = (x @ w_qkv).reshape(B, T, len(DIL_GROUPS), 3, DIL_HEADS, DIL_HEAD_DIM)
    slopes = alibi_slopes()
    parts, bufs = [], []
    for gi, (window, dilation) in enumerate(DIL_GROUPS):
        q, k, v = qkv[:, :, gi, 0], qkv[:, :, gi, 1], qkv[:, :, gi, 2]
        o, m, dn, nbuf = dilated_group_sample(q, k, v, bufs_in[gi], window, dilation, window // dilation, slopes)
        parts.append((o, m, dn))
        bufs.append(nbuf)
    o = merge_groups(parts).astype(x.dtype).reshape(B, T, DIL_HEADS * DIL_HEAD_DIM)
    return o @ w_o, bufs

def setup_inputs(seed: int = 0) -> dict:
    key = jax.random.key(seed)
    ks = jax.random.split(key, 24)
    f32 = jnp.float32
    n_pages = PAST_LEN // PAGE_SIZE
    n_used = DEC_BATCH * n_pages
    n_pool = n_used + n_used // 4

    def nrm(k, shape, scale=1.0):
        return jax.random.normal(k, shape, f32) * scale

    def gain(k, shape):
        return 1.0 + 0.01 * jax.random.normal(k, shape, f32)

    page_table = jax.random.permutation(ks[0], n_pool)[:n_used].reshape(DEC_BATCH, n_pages).astype(jnp.int32)
    dil_states = [nrm(ks[1 + gi], (N_DIL_LAYERS, DEC_BATCH, min(w, PAST_LEN), 2, DIL_HEADS, DIL_HEAD_DIM))
                  for gi, (w, d) in enumerate(DIL_GROUPS)]
    return {
        "x_prompt": nrm(ks[4], (BATCH, SEQ, D_MODEL)),
        "x_sample": nrm(ks[5], (DEC_BATCH, DEC_SEQ, D_MODEL)),
        "cache_mla_ckv": nrm(ks[6], (N_MLA_LAYERS, n_pool, PAGE_SIZE, MLA_KV_LORA)),
        "cache_mla_kpe": nrm(ks[7], (N_MLA_LAYERS, n_pool, PAGE_SIZE, MLA_ROPE)),
        "page_table": page_table,
        "state_dil_kv_w128": dil_states[0],
        "state_dil_kv_w512": dil_states[1],
        "state_dil_kv_w2048": dil_states[2],
        "mla_w_dq": nrm(ks[8], (N_MLA_LAYERS, D_MODEL, MLA_Q_LORA), D_MODEL ** -0.5),
        "mla_g_q": gain(ks[9], (N_MLA_LAYERS, MLA_Q_LORA)),
        "mla_w_uq": nrm(ks[10], (N_MLA_LAYERS, MLA_Q_LORA, MLA_HEADS * (MLA_NOPE + MLA_ROPE)), MLA_Q_LORA ** -0.5),
        "mla_w_dkv": nrm(ks[11], (N_MLA_LAYERS, D_MODEL, MLA_KV_LORA + MLA_ROPE), D_MODEL ** -0.5),
        "mla_g_kv": gain(ks[12], (N_MLA_LAYERS, MLA_KV_LORA)),
        "mla_w_uk": nrm(ks[13], (N_MLA_LAYERS, MLA_KV_LORA, MLA_HEADS, MLA_NOPE), MLA_KV_LORA ** -0.5),
        "mla_w_uv": nrm(ks[14], (N_MLA_LAYERS, MLA_KV_LORA, MLA_HEADS, MLA_VDIM), MLA_KV_LORA ** -0.5),
        "mla_w_o": nrm(ks[15], (N_MLA_LAYERS, MLA_HEADS * MLA_VDIM, D_MODEL), (MLA_HEADS * MLA_VDIM) ** -0.5),
        "dil_w_qkv": nrm(ks[16], (N_DIL_LAYERS, D_MODEL, len(DIL_GROUPS) * 3 * DIL_HEADS * DIL_HEAD_DIM), D_MODEL ** -0.5),
        "dil_w_o": nrm(ks[17], (N_DIL_LAYERS, DIL_HEADS * DIL_HEAD_DIM, D_MODEL), (DIL_HEADS * DIL_HEAD_DIM) ** -0.5),
        "norm_mix": gain(ks[18], (DEPTH, D_MODEL)),
        "norm_ffn": gain(ks[19], (DEPTH, D_MODEL)),
        "ffn_w_up": nrm(ks[20], (DEPTH, D_MODEL, D_FF), D_MODEL ** -0.5),
        "ffn_w_down": nrm(ks[21], (DEPTH, D_FF, D_MODEL), 0.5 * D_FF ** -0.5),
        "norm_final": gain(ks[22], (D_MODEL,)),
    }

def reference(x_prompt, x_sample, cache_mla_ckv, cache_mla_kpe, page_table,
              state_dil_kv_w128, state_dil_kv_w512, state_dil_kv_w2048,
              mla_w_dq, mla_g_q, mla_w_uq, mla_w_dkv, mla_g_kv, mla_w_uk, mla_w_uv, mla_w_o,
              dil_w_qkv, dil_w_o, norm_mix, norm_ffn, ffn_w_up, ffn_w_down, norm_final):
    dil_states = (state_dil_kv_w128, state_dil_kv_w512, state_dil_kv_w2048)
    xp, xs = x_prompt, x_sample
    ckv_p, kpe_p, ckv_s, kpe_s = [], [], [], []
    dil_p = [[] for _ in DIL_GROUPS]
    dil_s = [[] for _ in DIL_GROUPS]
    for layer in range(DEPTH):
        i = layer // N_MIXERS
        hp = rmsnorm(xp, norm_mix[layer])
        hs = rmsnorm(xs, norm_mix[layer])
        if layer % N_MIXERS == 0:
            w = (mla_w_dq[i], mla_g_q[i], mla_w_uq[i], mla_w_dkv[i], mla_g_kv[i], mla_w_uk[i], mla_w_uv[i], mla_w_o[i])
            yp, c_p, k_p = mla_prompt(hp, *w)
            ys, c_s, k_s = mla_sample(hs, cache_mla_ckv[i], cache_mla_kpe[i], page_table, *w)
            ckv_p.append(c_p); kpe_p.append(k_p); ckv_s.append(c_s); kpe_s.append(k_s)
        else:
            yp, bp = dil_prompt(hp, dil_w_qkv[i], dil_w_o[i])
            ys, bs = dil_sample(hs, [st[i] for st in dil_states], dil_w_qkv[i], dil_w_o[i])
            for gi in range(len(DIL_GROUPS)):
                dil_p[gi].append(bp[gi]); dil_s[gi].append(bs[gi])
        xp = xp + yp
        xs = xs + ys
        xp = xp + sqrelu_ffn(rmsnorm(xp, norm_ffn[layer]), ffn_w_up[layer], ffn_w_down[layer])
        xs = xs + sqrelu_ffn(rmsnorm(xs, norm_ffn[layer]), ffn_w_up[layer], ffn_w_down[layer])
    y_prompt = rmsnorm(xp, norm_final)
    y_sample = rmsnorm(xs, norm_final)
    return (y_prompt, y_sample,
            jnp.stack(ckv_p), jnp.stack(kpe_p), jnp.stack(ckv_s), jnp.stack(kpe_s),
            jnp.stack(dil_p[0]), jnp.stack(dil_p[1]), jnp.stack(dil_p[2]),
            jnp.stack(dil_s[0]), jnp.stack(dil_s[1]), jnp.stack(dil_s[2]))


_drawn_inputs = setup_inputs


def setup_inputs(seed=0):
    import zlib

    import numpy as np

    out = dict(_drawn_inputs(seed))
    spreads = {}
    factors = {'cache_mla_kpe': 3.712,
     'mla_g_q': 8.0,
     'mla_g_kv': 5.857,
     'norm_mix': 5.287,
     'norm_ffn': 7.055,
     'norm_final': 5.63}
    for name, (base, spread) in spreads.items():
        noise = np.random.default_rng([zlib.crc32(name.encode()), seed]).standard_normal(out[name].shape)
        drawn = base * np.exp(spread * noise) if base else spread * noise
        out[name] = __import__('jax').numpy.asarray(drawn.astype(out[name].dtype))
    for name, factor in factors.items():
        out[name] = (out[name] * factor).astype(out[name].dtype)
    return out
```

```python
from contextlib import ExitStack

import numpy as np

import concourse.bass as bass
from concourse import mybir

F32 = mybir.dt.float32
F32R = mybir.dt.float32r
I32 = mybir.dt.int32
ALU = mybir.AluOpType
ACT = mybir.ActivationFunctionType
AX = mybir.AxisListType.X

P = 128
NS = 8
NP = 512
T = NS + NP
HALF = T // 2
D = 1024
DT = D // P
FF = 4096
EPS = 1e-6
H, NOPE, ROPE, VD = 16, 64, 32, 64
QL, KVL = 384, 256
MLA_SCALE = float((NOPE + ROPE) ** -0.5)
PAST, PAGE = 4096, 128
GH, E = 8, 64
GROUPS = ((128, 1), (512, 4), (2048, 16))
DIL_SCALE = float(E ** -0.5)
KC = 8
MC = 256
WC = KC * MC
NB_T = NP // P
KPP = 8
NG = PAST // (P * KPP)
GR = 6
NEG = -1e30


class View:

    def __init__(self):
        self.n, self.per, self.i = {}, {}, None

    def at(self, name, back=0):
        base = self.n.get(name, 0) - back
        if self.i is not None and self.per.get(name):
            return self.i * self.per[name] + base
        return base

    def tick(self, name, k=1):
        self.n[name] = self.n.get(name, 0) + k
        return self.at(name)


def loop(eng, view, count, per, body):
    start = dict(view.n)
    with eng.Fori(0, count) as i:
        view.i, view.per = i, per
        body(i)
        view.i = None
    for name in set(view.n) | set(start):
        got = view.n.get(name, 0) - start.get(name, 0)
        assert got == per.get(name, 0), (name, got, per.get(name, 0))
        view.n[name] = start.get(name, 0) + count * got


def program(nc, io):
    with ExitStack() as ctx:
        def sb(name, shape, dt=F32, at=None):
            return (at or ctx).enter_context(nc.sbuf_tensor(name, shape, dt))

        xT = sb("xT", [P, DT, T])
        tmp = sb("tmp", [P, 4, T])
        rstd = sb("rstd", [P, T])
        wraw = sb("wraw", [P, 2, WC])
        whl = sb("whl", [P, 2, 2, WC], F32R)
        ident = sb("ident", [P, P])
        ones = sb("ones", [P, P])
        gains = sb("gains", [P, 5 * DT + 5])
        rope = sb("rope", [P, T])
        causal = sb("causal", [P, P])
        dist = sb("dist", [P, 1280])
        sdist = sb("sdist", [P, 3 * GH])
        half = sb("half", [P, 2, P])
        sq = sb("sq", [P, 2, T])
        mxs = sb("mxs", [P, 4])
        nbs = sb("nbs", [P, 4])
        den = sb("den", [P, 4])
        rden = sb("rden", [P, 4])

        idx = sb("idx", [P, NS * NG], I32)
        pti = sb("pti", [NS * NG, 8], I32)
        ptf = sb("ptf", [NS * NG, 8], F32)
        ptT = sb("ptT", [8, NS * NG], F32)
        sel = sb("sel", [8, P], F32)
        poff = sb("poff", [P, 1], F32)
        ctxH = ExitStack()
        hA = sb("hA", [P, DT, 2, T], F32R, ctxH)
        cx = ExitStack()
        uT = sb("uT", [P, 16, 2, T], F32R, cx)
        cx.close()
        cx = ExitStack()
        yn = sb("yn", [P, NB_T + 1, D], F32, cx)
        cx.close()
        cx = ExitStack()
        xin = sb("xin", [P, NB_T, D], F32, cx)
        xsin = sb("xsin", [NS, D], F32, cx)
        cx.close()
        cm = ExitStack()
        ckvT = sb("ckvT", [P, 2, T], F32, cm)
        kpeT = sb("kpeT", [P, T], F32, cm)
        qS = sb("qS", [96, H, NS], F32, cm)
        qlat = sb("qlat", [P, NS, 2, H], F32, cm)
        bd = sb("bd", [P, NS, 4, H], F32, cm)
        oS = sb("oS", [P, DT, NS], F32, cm)
        olat = sb("olat", [P, 2, H, NS], F32, cm)
        cx = ExitStack()
        ckvH = sb("ckvH", [P, 2, 2, T], F32R, cx)
        cq = sb("cq", [P, 3, T], F32, cx)
        v = sb("v", [P, NB_T, H * VD], F32, cx)
        cx2 = ExitStack()
        natc = sb("natc", [P, NB_T + 1, KVL + ROPE], F32, cx2)
        cx2.close()
        cx2 = ExitStack()
        onat = sb("onat", [P, NB_T, H * VD], F32, cx2)
        qh = sb("qh", [96, 4, T], F32, cx2)
        kh = sb("kh", [96, 4, NP], F32, cx2)
        pr = sb("pr", [P, 2, NP], F32, cx2)
        pT = sb("pT", [P, 2, NP], F32, cx2)
        rt = sb("rt", [96, 2, T], F32, cx2)
        cx2.close()
        cx.close()
        cx = ExitStack()
        gat = sb("gat", [P, GR, KPP * KVL], F32, cx)
        gkp = sb("gkp", [P, GR, KPP * ROPE], F32, cx)
        cx2 = ExitStack()
        wukT = sb("wukT", [NOPE, H, KVL], F32, cx2)
        cx2.close()
        cT = sb("cT", [P, 2, 4, 2, P], F32, cx)
        kT4 = sb("kT4", [P, 2, P], F32, cx)
        psm = sb("psm", [P, 33 * H], F32, cx)
        wuv = sb("wuv", [P, 2, H * VD], F32, cx)
        mb = sb("mb", [P, 2, H], F32, cx)
        sm = sb("sm", [P, H], F32, cx)
        cx.close()
        cm.close()
        cx = ExitStack()
        sN = sb("sN", [P, 3, GH, NS], F32, cx)
        vS = sb("vS", [P, 3, 4, NS], F32, cx)
        prodS = sb("prodS", [P, 3, 4, NS], F32, cx)
        oSd = sb("oSd", [P, 4, NS], F32, cx)
        dq = sb("dq", [P, 3, 4, T], F32, cx)
        dk = sb("dk", [P, 3, 4, T], F32, cx)
        dv = sb("dv", [P, 3, NB_T, GH * E], F32, cx)
        nat = sb("nat", [P, 2, GH * E], F32, cx)
        cx.close()
        cx = ExitStack()
        sb("kept", [P, 3 * GH * NS + 2 * 3 * 4 * NS + 4 * NS], F32, cx)
        kv = sb("kv", [P, 6, GH * E], F32, cx)
        qb = sb("qb", [P, 2, 3 * GH * E], F32, cx)
        pv_ = sb("pv_", [P, 2, GH * E], F32, cx)
        sS = sb("sS", [P, 3, NS, GH], F32, cx)
        mS = sb("mS", [P, 4, NS * GH], F32, cx)
        cx.close()
        ctxH.close()
        cx = ExitStack()
        sc = sb("sc", [P, 2, 1280], F32, cx)
        scT = sb("scT", [P, 4, 4 * P], F32, cx)
        ond = sb("ond", [P, NB_T, GH * E], F32, cx)
        cx.close()

        ps = ctx.enter_context(nc.psum_tensor("ps", [P, 8, 512], F32))

        unit = ps[:].rearrange("p (u a) n -> p u a n", a=2)

        def cols(t, f):
            sl = bass.ds(f, 1) if not isinstance(f, int) else slice(f, f + 1)
            return t[:, sl, :].rearrange("p f (a b) -> p f a b", a=2)

        def part(t, f, hl):
            sl = bass.ds(f, 1) if not isinstance(f, int) else slice(f, f + 1)
            return t[:, sl, hl, :]

        mark = {}

        def semaphore(name):
            return ctx.enter_context(nc.semaphore(name))

        tokens_in = semaphore("tokens_in")
        constants_in = semaphore("constants_in")
        pages_in = semaphore("pages_in")
        chunk_high = semaphore("chunk_high")
        chunk_low = semaphore("chunk_low")
        first_chunk_used = semaphore("first_chunk_used")
        tile_summed = semaphore("tile_summed")
        tile_taken = semaphore("tile_taken")
        tile_ready = semaphore("tile_ready")
        tile_high = semaphore("tile_high")
        tile_low = semaphore("tile_low")
        squares_ready = semaphore("squares_ready")
        squares_used = semaphore("squares_used")
        inverse_ready = semaphore("inverse_ready")
        root_ready = semaphore("root_ready")
        pages_ready = semaphore("pages_ready")
        scores_ready = semaphore("scores_ready")
        max_ready = semaphore("max_ready")
        exponents_ready = semaphore("exponents_ready")
        probs_ready = semaphore("probs_ready")
        turned_ready = semaphore("turned_ready")
        turned_taken = semaphore("turned_taken")
        output_ready = semaphore("output_ready")
        reciprocal_ready = semaphore("reciprocal_ready")
        output_taken = semaphore("output_taken")
        values_used = semaphore("values_used")
        dil_scores_taken = semaphore("dil_scores_taken")
        max_spread = semaphore("max_spread")
        wuk_in = semaphore("wuk_in")
        wuv_in = semaphore("wuv_in")
        rotary_ready = semaphore("rotary_ready")
        gather_used = semaphore("gather_used")
        keys_turned = semaphore("keys_turned")
        keys_taken = semaphore("keys_taken")
        keys_used = semaphore("keys_used")
        products_ready = semaphore("products_ready")
        cached_used = semaphore("cached_used")
        final_ready = semaphore("final_ready")
        dve_step = semaphore("dve_step")
        latents_stored = semaphore("latents_stored")
        rows_stored = semaphore("rows_stored")
        states_copied = semaphore("states_copied")
        chunk_in = [semaphore(f"chunk_in{i}") for i in range(2)]
        nat_stored = [semaphore(f"nat_stored{i}") for i in range(2)]
        gather_in = [semaphore(f"gather_in{i}") for i in range(GR)]
        cached_in = [semaphore(f"cached_in{i}") for i in range(6)]
        queries_in = [semaphore(f"queries_in{i}") for i in range(2)]

        def row0(gi, t):
            return t * P - (NP - min(GROUPS[gi][0], NP))

        def kept_tiles(gi):
            return [t for t in range(NB_T) if row0(gi, t) >= 0]

        NI = H * NB_T
        PROJECT = (2, 4, 6)

        NAT_ROWS = sum(3 + len(kept_tiles(gi)) for gi in range(3))
        NATS = [(NAT_ROWS + 1) // 2, NAT_ROWS // 2]
        ST_V = sum(len(kept_tiles(gi)) for gi in range(3))

        M1 = (H + GH) * NB_T + 3 * NS

        def due(count):
            return not isinstance(count, int) or count > 0

        def full(slot):
            return [(lambda hl: whl[:, slot, hl, :], wraw[:, slot, :])]

        def narrow(slot):
            return [(lambda hl: whl[:, slot, hl, 0:KC * P], wraw[:, slot, 0:KC * P])]

        def swapped(out, raw, rope0):
            hr = ROPE // 2
            return [(lambda hl: out(hl)[..., P - ROPE - raw.shape[-1]:P - ROPE], raw),
                    (lambda hl: out(hl)[..., P - ROPE:P - hr], raw[..., rope0 + hr:rope0 + ROPE]),
                    (lambda hl: out(hl)[..., P - hr:P], raw[..., rope0:rope0 + hr])]

        def rotary(slot):
            return swapped(lambda hl: whl[:, slot, hl, 0:KC * P].rearrange("p (k m) -> p k m", k=KC),
                           wraw[:, slot, 0:KC * ROPE].rearrange("p (k m) -> p k m", k=KC), 0)

        def pair(slot):
            nq = 3 * 2 * (NOPE + ROPE)
            return swapped(lambda hl: whl[:, slot, hl, 0:3 * MC].rearrange("p (k m) -> p k m", m=P),
                           wraw[:, slot, 0:nq].rearrange("p (k m) -> p k m", m=NOPE + ROPE), NOPE) + \
                [(lambda hl: whl[:, slot, hl, 3 * MC:3 * MC + 2 * P], wraw[:, slot, nq:nq + 2 * P])]

        KINDS = [full, narrow, full, rotary, full] + [pair] * (H // 2)
        PIECES = {narrow: 1, full: 1, rotary: 1, pair: 2}

        def n_parts(t):
            return -(-(min(t + 1, 2) + 2 * (t + 1)) // 4)

        block = ctx.enter_context(nc.Block())

        @block.tensor
        def _(pe):
            vw = View()

            def z_begin(u=None, every=False):
                if every:
                    pe.wait_ge(tile_taken, vw.at("tile_summed"))
                else:
                    if due(vw.at("tile_summed", 3)):
                        pe.wait_ge(tile_taken, vw.at("tile_summed", 3))
                return vw.n.get("tile_summed", 0) % 4 if u is None else u

            def z_end(ins):
                ins.then_inc(tile_summed, 1)
                vw.tick("tile_summed")

            def w_begin():
                slot = vw.n.get("w", 0) % 2
                pe.wait_ge(chunk_low, vw.tick("w"))
                return slot

            def whole(u, hi, lo, rhs, ks, start=True, stop=True):
                for n, k in enumerate(ks):
                    first, last = start and n == 0, stop and n == len(ks) - 1
                    for a in range(2):
                        c = slice(a * HALF, (a + 1) * HALF)
                        pe.matmul(ps[:, 2 * u + a, 0:HALF], hi(k), rhs(k, 0)[:, c], start=first, stop=False)
                        pe.matmul(ps[:, 2 * u + a, 0:HALF], hi(k), rhs(k, 1)[:, c], start=False, stop=False)
                    for a in range(2):
                        c = slice(a * HALF, (a + 1) * HALF)
                        ins = pe.matmul(ps[:, 2 * u + a, 0:HALF], lo(k), rhs(k, 0)[:, c], start=False, stop=last)
                return ins

            def wparts(slot, off, nk, m):
                return [whl[:, slot, hl, off:off + nk * m].rearrange("p (k m) -> p k m", k=nk) for hl in range(2)]

            def linear(nk, m_tiles, m, rhs):
                slot = w_begin()
                hi, lo = wparts(slot, 0, nk, m)
                for mt in range(m_tiles):
                    u = z_begin()
                    c = slice(mt * P, (mt + 1) * P)
                    ins = whole(u, lambda k: hi[:, k, c], lambda k: lo[:, k, c], rhs, range(nk))
                    z_end(ins)

            def norm_sum(nt):
                u = z_begin()
                for f in range(nt):
                    n = vw.tick("squares_ready")
                    pe.wait_ge(squares_ready, n)
                    for a in range(2):
                        ins = pe.matmul(ps[:, 2 * u + a, 0:HALF], ones[:], sq[:, (n - 1) % 2, a * HALF:(a + 1) * HALF],
                                        start=(f == 0), stop=(f == nt - 1))
                    if f < nt - 1:
                        ins.then_inc(squares_used, 1)
                z_end(ins)

            def split_ready(n):
                pe.wait_ge(tile_low, vw.tick("a", n))

            hA_k = lambda k, hl: hA[:, k, hl, :]

            pe.wait_ge(constants_in, 16 * 10)
            pe.wait_ge(tokens_in, 32)
            for f in range(DT):
                if f % 2 == 0:
                    u = z_begin()
                for t in range(NB_T):
                    ins = pe.transpose(ps[:, f, t * P:(t + 1) * P], xin[:, t, f * P:(f + 1) * P], ident[:])
                if f % 2:
                    z_end(ins)
            u = z_begin()
            for f in range(DT):
                ins = pe.transpose(ps[:, 2 * u, f * NS:(f + 1) * NS], xsin[:, f * P:(f + 1) * P], ident[0:NS, 0:NS])
            z_end(ins)

            norm_sum(DT)
            split_ready(DT)
            linear(KC, 2, MC, hA_k)
            linear(KC, 1, P, hA_k)
            linear(KC, 2, MC, hA_k)
            linear(KC, 1, P, hA_k)
            norm_sum(3)
            norm_sum(2)
            split_ready(5)
            pe.wait_ge(pages_ready, 1)
            u = z_begin()
            z_end(pe.transpose(ps[0:8, 2 * u, 0:NS * NG], ptf[:], ident[0:NS * NG, 0:NS * NG]))
            pe.wait_ge(tile_taken, vw.at("tile_summed"))
            u = z_begin()
            z_end(pe.matmul(ps[:, 2 * u, 0:NS * NG], sel[:], ptT[:], start=True, stop=True))
            mark["idx"] = vw.at("tile_summed")
            slot = w_begin()
            hi, lo = wparts(slot, 0, 2, H * VD)
            for t in range(NB_T):
                u = z_begin()
                tok = slice(NS + t * P, NS + (t + 1) * P)
                for a in range(2):
                    c = slice(a * 512, (a + 1) * 512)
                    for k in range(2):
                        pe.matmul(ps[:, 2 * u + a, :], ckvH[:, k, 0, tok], hi[:, k, c], start=(k == 0), stop=False)
                        pe.matmul(ps[:, 2 * u + a, :], ckvH[:, k, 0, tok], lo[:, k, c], start=False, stop=False)
                        ins = pe.matmul(ps[:, 2 * u + a, :], ckvH[:, k, 1, tok], hi[:, k, c], start=False, stop=(k == 1))
                z_end(ins)
            for t in range(NB_T + 1):
                u = z_begin()
                tok = slice(0, NS) if t == NB_T else slice(NS + t * P, NS + (t + 1) * P)
                n = tok.stop - tok.start
                for k in range(2):
                    pe.transpose(ps[0:n, 2 * u, k * P:(k + 1) * P], ckvT[:, k, tok], ident[:])
                z_end(pe.transpose(ps[0:n, 2 * u, KVL:KVL + ROPE], kpeT[64:96, tok], ident[64:96, 64:96]))
            mark["latents"] = vw.at("tile_summed")

            slot_ = [0]

            def project(step):
                if step == 0:
                    slot_[0] = w_begin()
                u = z_begin(3, every=True)
                if step < 2:
                    hi, lo = wparts(slot_[0], 0, 3, MC)
                    c = slice(step * P, (step + 1) * P)
                    ins = whole(u, lambda k: hi[:, k, c], lambda k: lo[:, k, c], hA_k, range(3))
                else:
                    hi, lo = wparts(slot_[0], 3 * MC, 2, P)
                    for k in range(2):
                        pe.matmul(ps[:, 2 * u, :], hi[:, k, :], ckvH[:, k, 0, NS:], start=(k == 0), stop=False)
                        pe.matmul(ps[:, 2 * u, :], hi[:, k, :], ckvH[:, k, 1, NS:], start=False, stop=False)
                        ins = pe.matmul(ps[:, 2 * u, :], lo[:, k, :], ckvH[:, k, 0, NS:], start=False, stop=(k == 1))
                z_end(ins)

            def scores(i):
                h, t = i // NB_T, i % NB_T
                if due(i - 1):
                    pe.wait_ge(probs_ready, i - 1)
                tok = slice(NS + t * P, NS + (t + 1) * P)
                pe.matmul(ps[:, i % 2, 0:(t + 1) * P], qh[:, h % 4, tok], kh[:, h % 4, 0:(t + 1) * P],
                          start=True, stop=True).then_inc(scores_ready, 1)

            def turn(i):
                t = i % NB_T
                pe.wait_ge(probs_ready, i + 1)
                if due(i - 1):
                    pe.wait_ge(turned_taken, i - 1)
                for b in range(t + 1):
                    ins = pe.transpose(ps[:, 2 + i % 2, b * P:(b + 1) * P], pr[:, i % 2, b * P:(b + 1) * P], ident[:])
                ins.then_inc(turned_ready, 1)

            def values(i):
                h, t = i // NB_T, i % NB_T
                pe.wait_ge(turned_taken, i + 1)
                if due(i - 1):
                    pe.wait_ge(output_taken, i - 1)
                for b in range(t + 1):
                    ins = pe.matmul(ps[:, 4 + i % 2, 0:VD], pT[:, i % 2, b * P:(b + 1) * P],
                                    v[:, b, h * VD:(h + 1) * VD], start=(b == 0), stop=(b == t))
                ins.then_inc(output_ready, 1)

            pe.wait_ge(tile_taken, vw.at("tile_summed"))
            for step in range(3):
                project(step)
            for i in range(NI + 2):
                if i % 8 in PROJECT and i < NI - 8:
                    project(PROJECT.index(i % 8))
                if i % 8 == 0 and i < NI:
                    pe.wait_ge(tile_taken, vw.at("tile_summed"))
                if i < NI:
                    scores(i)
                if 1 <= i <= NI:
                    turn(i - 1)
                if i >= 2:
                    values(i - 2)
            pe.wait_ge(output_taken, NI)

            for f in range(DT):
                u = z_begin()
                for t in range(NB_T):
                    ins = pe.transpose(ps[:, 2 * u, t * P:(t + 1) * P], onat[:, t, f * P:(f + 1) * P], ident[:])
                z_end(ins)
            mark["onat"] = vw.at("tile_summed")
            pe.wait_ge(wuk_in, 16)
            wuk = gat[:, GR - 1, :].rearrange("p (k h n) -> p k h n", k=2, h=H)
            for q4 in range(4):
                u = z_begin()
                for hh in range(4):
                    for k in range(2):
                        col = (hh * 2 + k) * P
                        ins = pe.transpose(ps[0:NOPE, 2 * u + col // 512, col % 512:col % 512 + P],
                                           wuk[:, k, 4 * q4 + hh, :], ident[:])
                z_end(ins)
            pe.wait_ge(tile_taken, vw.at("tile_summed"))
            u = z_begin()
            for k in range(2):
                for h in range(H):
                    ins = pe.matmul(ps[:, 2 * u + k, h * NS:(h + 1) * NS], wukT[:, h, k * P:(k + 1) * P],
                                    qS[0:NOPE, h, :], start=(h == 0), stop=(h == H - 1), skip_group_check=True)
            z_end(ins)
            mark["qlat"] = vw.at("tile_summed")
            pe.wait_ge(tile_taken, vw.at("tile_summed"))
            pe.wait_ge(rotary_ready, 1)
            def turn_keys(m):
                g, q = m // 2, m % 2
                if q == 0:
                    pe.wait_ge(gather_in[g % GR], 32 * (g // GR + 1))
                gv = gat[:, g % GR, :].rearrange("p (s k c) -> p s k c", s=KPP, k=2)
                for hf in range(2):
                    if due(3 * (m - 1) + hf + 1):
                        pe.wait_ge(keys_taken, 3 * (m - 1) + hf + 1)
                    for s_ in range(2):
                        for k in range(2):
                            ins = pe.transpose(ps[:, hf, (s_ * 2 + k) * P:(s_ * 2 + k + 1) * P],
                                               gv[:, q * 4 + hf * 2 + s_, k, :], ident[:])
                    ins.then_inc(keys_turned, 1)
                if due(3 * m):
                    pe.wait_ge(keys_taken, 3 * m)
                pe.transpose(ps[:, 2, 0:P], gkp[:, g % GR, q * P:(q + 1) * P], ident[:]).then_inc(keys_turned, 1)

            def score_keys(m):
                b, q8 = m // 8, m % 8
                if q8 == 0 and b >= 2:
                    pe.wait_ge(probs_ready, NI + b - 1)
                pe.wait_ge(keys_taken, 3 * (m + 1))
                sbank = 4 + b % 2
                pe.matmul(ps[:, sbank, q8 * 64:(q8 + 1) * 64], kT4[:, m % 2, :], bd[:, b, :, :].rearrange("p s h -> p (s h)"),
                          start=(q8 == 0), stop=False, skip_group_check=True)
                for s_ in range(4):
                    for k in range(2):
                        ins = pe.matmul(ps[:, sbank, q8 * 64 + s_ * H:q8 * 64 + (s_ + 1) * H], cT[:, m % 2, s_, k, :],
                                        qlat[:, b, k, :], start=False, stop=(q8 == 7 and s_ == 3 and k == 1),
                                        skip_group_check=True)
                ins.then_inc(keys_used, 1)

            def score_new(b):
                pe.wait_ge(probs_ready, NI + b)
                pe.matmul(ps[:, 6, 0:H], kpeT[64:96, b:b + 1].to_broadcast([ROPE, P]), bdq(b), start=True, stop=False)
                for k in range(2):
                    ins = pe.matmul(ps[:, 6, 0:H], ckvT[:, k, b:b + 1].to_broadcast([P, P]), qlat[:, b, k, :],
                                    start=False, stop=(k == 1))
                ins.then_inc(scores_ready, 1)

            def bdq(b):
                return bd[64:96, b, 2, :]

            def max_rows(b):
                pe.wait_ge(max_ready, NI + 3 * b + 1)
                pe.transpose(ps[0:H, 3, 0:P], mb[:, 0, :], ident[:]).then_inc(max_spread, 1)

            def max_all(b):
                pe.wait_ge(max_ready, NI + 3 * b + 2)
                pe.matmul(ps[:, 3, 128:128 + H], ones[0:H, :], sm[0:H, :], start=True, stop=True).then_inc(max_spread, 1)

            def out_keys(b):
                pe.wait_ge(probs_ready, NI + b + 1)
                pe.wait_ge(output_taken, NI + b)
                for c in range(4 * KPP):
                    g = b * NG + c // KPP
                    gv = gat[:, g % GR, :].rearrange("p (s k c) -> p s k c", s=KPP, k=2)
                    for k in range(2):
                        ins = pe.matmul(ps[:, 7, k * H:(k + 1) * H], gv[:, c % KPP, k, :], psm[:, c * H:(c + 1) * H],
                                        start=(c == 0 and k == 0), stop=(c == 4 * KPP - 1), skip_group_check=True)
                    if c % KPP == KPP - 1:
                        ins.then_inc(gather_used, 1)
                pe.wait_ge(max_ready, NI + 3 * b + 3)
                pe.matmul(ps[:, 7, 2 * H:3 * H], ones[:], mb[:, 1, :], start=False, stop=True,
                          skip_group_check=True).then_inc(output_ready, 1)

            NM = NS * 8
            turn_keys(0)
            for b in range(NS):
                for q8 in range(8):
                    m = b * 8 + q8
                    if q8 == 1 and b:
                        max_rows(b - 1)
                    if m + 1 < NM:
                        turn_keys(m + 1)
                    score_keys(m)
                    if q8 == 1 and b:
                        max_all(b - 1)
                    if q8 == 2 and b:
                        out_keys(b - 1)
                score_new(b)
            max_rows(NS - 1)
            max_all(NS - 1)
            out_keys(NS - 1)
            pe.wait_ge(wuv_in, 16)
            pe.wait_ge(output_taken, NI + NS)
            u = z_begin()
            for h in range(H):
                r = (h % 2) * VD
                for k in range(2):
                    ins = pe.matmul(ps[r:r + VD, 2 * u, (h // 2) * NS:(h // 2 + 1) * NS], wuv[:, k, h * VD:(h + 1) * VD],
                                    olat[:, k, h, :], start=(k == 0), stop=(k == 1), skip_group_check=True)
            z_end(ins)
            split_ready(DT + 1)
            for c in range(4):
                linear(KC, 2, MC, hA_k)

            def mlp():
                norm_sum(DT)
                split_ready(DT)
                for hf in range(2):
                    loop(pe, vw, 4, {"w": 2, "tile_summed": 4}, lambda i: [linear(KC, 2, MC, hA_k) for _ in range(2)])
                    split_ready(16)

                    def down(i):
                        for m in range(2):
                            us = None
                            for kk in range(2):
                                slot = w_begin()
                                hi, lo = wparts(slot, 0, KC, MC)
                                if kk == 0:
                                    pe.wait_ge(tile_taken, vw.at("tile_summed", 2))
                                    us = [(vw.n["tile_summed"] + mt) % 4 for mt in range(2)]
                                for mt in range(2):
                                    c = slice(mt * P, (mt + 1) * P)
                                    ins = whole(us[mt], lambda k: hi[:, k, c], lambda k: lo[:, k, c],
                                                lambda k, hl: uT[:, kk * KC + k, hl, :], range(KC),
                                                start=(kk == 0), stop=(kk == 1))
                                    if kk == 1 and mt == 0:
                                        ins.then_inc(tile_summed, 1)
                                ins.then_inc(tile_summed if kk else first_chunk_used, 1)
                            vw.tick("tile_summed", 2)
                    loop(pe, vw, 2, {"w": 4, "tile_summed": 4}, down)

            mlp()

            norm_sum(DT)
            split_ready(DT)

            def to_rows(src, n, gi):
                u = z_begin()
                for f in range(4):
                    ins = pe.transpose(ps[0:n, 2 * u, f * P:(f + 1) * P], src(f), ident[:])
                z_end(ins)
                mark.setdefault("rows", []).append(vw.at("tile_summed"))

            for gi in range(3):
                for part_ in range(3):
                    for c in range(2):
                        linear(KC, 2, MC, hA_k)
                    pe.wait_ge(tile_taken, vw.at("tile_summed"))
                    src = (dq, dk, None)[part_]
                    def get(f, c):
                        return tmp[:, f, c] if src is None else src[:, gi, f, c]
                    to_rows(lambda f: get(f, slice(0, NS)), NS, gi)
                    for t in (kept_tiles(gi) if part_ == 1 else range(NB_T) if part_ == 2 else []):
                        to_rows(lambda f: get(f, slice(NS + t * P, NS + (t + 1) * P)), P, gi)
            pe.wait_ge(products_ready, 1)
            u = z_begin()
            for hp in range(2):
                ins = pe.matmul(ps[:, 2 * u, hp * 96:(hp + 1) * 96], half[:, hp, :],
                                prodS[:].rearrange("p g t b -> p (g t b)"), start=(hp == 0), stop=True,
                                skip_group_check=True)
            z_end(ins)
            pe.wait_ge(tile_taken, vw.at("tile_summed"))

            DI = GH * NB_T
            P0, T0, O0 = NI + NS, NI, NI + NS

            def d_scores(i):
                h, t = i // NB_T, i % NB_T
                if due(i - 1):
                    pe.wait_ge(dil_scores_taken, i - 1)
                if i >= 2:
                    pe.wait_ge(output_taken, O0 + i - 1)
                r = (h % 2) * E
                q_ = lambda g: dq[r:r + E, g, h // 2, NS + t * P:NS + (t + 1) * P]
                base = 3 * (i % 2)
                for g in range(3):
                    k0 = max(t - 1, 0) if g == 0 else 0
                    ins = pe.matmul(ps[:, base + g, 0:(t + 1 - k0) * P], q_(g),
                                    dk[r:r + E, g, h // 2, NS + k0 * P:NS + (t + 1) * P], start=True, stop=True)
                ins.then_inc(scores_ready, 1)

            def d_blocks(i):
                t = i % NB_T
                return [(0, b) for b in range(max(t - 1, 0), t + 1)] + [(g, b) for g in (1, 2) for b in range(t + 1)]

            tn = [0]
            un = [0]

            def d_turn(i, part_):
                blocks = d_blocks(i)[4 * part_:4 * part_ + 4]
                n = tn[0]
                pe.wait_ge(turned_taken, T0 + n - 1)
                for b in range(len(blocks)):
                    c = (4 * part_ + b) * P
                    ins = pe.transpose(ps[:, 6 + n % 2, b * P:(b + 1) * P], sc[:, i % 2, c:c + P], ident[:])
                ins.then_inc(turned_ready, 1)
                tn[0] += 1

            def d_values(i, part_):
                h = i // NB_T
                blocks = d_blocks(i)
                n = un[0]
                pe.wait_ge(turned_taken, T0 + n + 1)
                for b, (g, kb) in enumerate(blocks[4 * part_:4 * part_ + 4]):
                    ins = pe.matmul(ps[:, 3 * (i % 2), 256:256 + E], scT[:, n % 4, b * P:(b + 1) * P],
                                    dv[:, g, kb, h * E:(h + 1) * E], start=(part_ == 0 and b == 0),
                                    stop=(4 * part_ + b == len(blocks) - 1))
                ins.then_inc(values_used, 1)
                un[0] += 1

            d_scores(0)
            d_scores(1)
            for i in range(DI):
                parts = -(-len(d_blocks(i)) // 4)
                pe.wait_ge(probs_ready, P0 + i + 1)
                d_turn(i, 0)
                for k in range(parts):
                    if k + 1 < parts:
                        d_turn(i, k + 1)
                    d_values(i, k)
                if i + 2 < DI:
                    d_scores(i + 2)
            pe.wait_ge(output_taken, O0 + DI)

            pe.wait_ge(max_ready, M1 + 1)
            pe.transpose(ps[0:64, 0, 0:P], mS[:, 0, :], ident[:]).then_inc(max_spread, 1)
            pe.wait_ge(max_ready, M1 + 2)
            pe.matmul(ps[:, 1, 0:64], ones[0:64, :], mS[0:64, 1, :], start=True, stop=True).then_inc(max_spread, 1)
            pe.wait_ge(max_ready, M1 + 3)
            pe.matmul(ps[:, 2, 0:64], ones[:], mS[:, 3, :], start=True, stop=True).then_inc(max_spread, 1)
            for n in range(3 * NS, 6 * NS):
                b, gi = (n - 3 * NS) // 3, n % 3
                pe.wait_ge(cached_in[n % 6], 16 * (n // 6 + 1))
                for f in range(4):
                    c = (b * 4 + f) * GH
                    ins = pe.matmul(ps[:, 4, c:c + GH], kv[:, n % 6, f * P:(f + 1) * P], sS[:, gi, b, :],
                                    start=(gi == 0 and f == 0 and b == 0), stop=(gi == 2), skip_group_check=True)
                ins.then_inc(cached_used, 1)
            pe.wait_ge(tile_taken, vw.at("tile_summed"))
            pe.wait_ge(output_taken, O0 + DI + 1)
            for f in range(4):
                u = z_begin()
                for t in range(NB_T):
                    ins = pe.transpose(ps[:, 2 * u, t * P:(t + 1) * P], ond[:, t, f * P:(f + 1) * P], ident[:])
                z_end(ins)
            split_ready(4)
            for c in range(2):
                linear(4, 4, 2 * MC, hA_k)
            mlp()
            norm_sum(DT)
            for f in range(DT):
                pe.wait_ge(final_ready, f + 1)
                u = z_begin()
                for t in range(NB_T):
                    pe.transpose(ps[:, 2 * u, t * P:(t + 1) * P], tmp[:, f % 4, NS + t * P:NS + (t + 1) * P], ident[:])
                z_end(pe.transpose(ps[0:NS, 2 * u + 1, 0:P], tmp[:, f % 4, 0:NS], ident[:]))
            mark["last"] = vw.at("tile_summed")

        @block.sync
        def _(sp):
            vw = View()
            copied = [0]

            def chunk(*pairs):
                vw.tick("w")
                slot = (vw.n["w"] - 1) % 2
                if due(vw.at("w", 2)):
                    sp.wait_ge(chunk_low, vw.at("w", 2))
                for off, (a, b), src in pairs:
                    dst = wraw[:, slot, off:off + a * b].rearrange("p (a b) -> p a b", a=a)
                    sp.dma_start(dst, src).then_inc(chunk_in[slot], 16)

            def wsrc(w, k0, k, c0, c):
                return w[k0 * P:(k0 + k) * P, :].rearrange("(k p) m -> p k m", p=P)[:, :, c0:c0 + c] \
                    if isinstance(c0, int) else \
                    w[k0 * P:(k0 + k) * P, :].rearrange("(k p) m -> p k m", p=P)[:, :, bass.ds(c0, c)]

            def state_copies():
                for gi, (w, d) in enumerate(GROUPS):
                    wb = min(w, PAST)
                    cuts = 4 if wb > 1024 else 1
                    run = (wb - 1) * 2 * GH * E // 16 // cuts
                    for b in range(NS):
                        src = io["state"][gi][b, 1:wb].rearrange("r c -> (r c)").rearrange(
                            "(u a n) -> u a n", u=cuts, a=16)
                        dst = io["ds"][gi][b, 0:wb - 1].rearrange("r c -> (r c)").rearrange(
                            "(u a n) -> u a n", u=cuts, a=16)
                        for u in range(cuts):
                            yield dst[u], src[u]

            copies = list(state_copies())

            def copy_some(n):
                for _ in range(n):
                    if copied[0] < len(copies):
                        dst, src = copies[copied[0]]
                        sp.dma_start(dst, src).then_inc(states_copied, 16)
                        copied[0] += 1

            sp.dma_start(xin[:], io["xp"].rearrange("(t p) d -> p t d", p=P)).then_inc(tokens_in, 16)
            sp.dma_start(xsin[:], io["xs"]).then_inc(tokens_in, 16)
            for dst, name in ((ident, "ident"), (ones, "ones"), (gains, "gains"), (rope, "rope"),
                              (causal, "causal"), (dist, "dist"), (sdist, "sdist")):
                sp.dma_start(dst[:], io[name]).then_inc(constants_in, 16)
            sp.dma_start(half[:], io["half"].rearrange("p (a b) -> p a b", a=2)).then_inc(constants_in, 16)
            sp.dma_start(sel[:], io["sel"]).then_inc(constants_in, 16)
            sp.dma_start(poff[:], io["poff"]).then_inc(constants_in, 16)
            sp.dma_start(pti[:], io["pt"]).then_inc(pages_in, 16)
            chunk((0, (KC, MC), wsrc(io["w_dq"], 0, KC, 0, MC)))
            chunk((0, (KC, P), wsrc(io["w_dq"], 0, KC, MC, P)))
            chunk((0, (KC, MC), wsrc(io["w_dkv"], 0, KC, 0, MC)))
            chunk((0, (KC, ROPE), wsrc(io["w_dkv"], 0, KC, KVL, ROPE)))
            chunk((0, (2, H * VD), wsrc(io["w_uv"], 0, 2, 0, H * VD)))
            hd = 2 * (NOPE + ROPE)
            for j in range(H // 2):
                chunk((0, (3, hd), wsrc(io["w_uq"], 0, 3, j * hd, hd)),
                      (3 * hd, (2, P), wsrc(io["w_uk"], 0, 2, j * P, P)))
                if j == 1:
                    sp.wait_ge(tile_taken, mark["latents"])
                    sp.dma_start(io["ckv_p"].rearrange("(t p) c -> p t c", p=P), natc[:, 0:NB_T, 0:KVL]).then_inc(latents_stored, 16)
                    sp.dma_start(io["kpe_p"].rearrange("(t p) c -> p t c", p=P), natc[:, 0:NB_T, KVL:]).then_inc(latents_stored, 16)
                    sp.dma_start(io["ckv_s"], natc[0:NS, NB_T, 0:KVL]).then_inc(latents_stored, 16)
                    sp.dma_start(io["kpe_s"], natc[0:NS, NB_T, KVL:]).then_inc(latents_stored, 16)
                copy_some(1)
            chunk((0, (KC, MC), wsrc(io["w_omla"], 0, KC, 0, MC)))
            chunk((0, (KC, MC), wsrc(io["w_omla"], 0, KC, MC, MC)))
            sp.wait_ge(tile_taken, mark["onat"])
            sp.dma_start(gat[:, GR - 1, :].rearrange("p (a b) -> p a b", a=2),
                         wsrc(io["w_uk"], 0, 2, 0, H * NOPE)).then_inc(wuk_in, 16)
            sp.wait_ge(tile_taken, mark["qlat"])
            sp.dma_start(wuv[:], wsrc(io["w_uv"], 0, 2, 0, H * VD)).then_inc(wuv_in, 16)
            copy_some(8)
            chunk((0, (KC, MC), wsrc(io["w_omla"], 0, KC, 2 * MC, MC)))
            chunk((0, (KC, MC), wsrc(io["w_omla"], 0, KC, 3 * MC, MC)))

            def mlp(layer):
                up, down = io["w_up"][layer], io["w_down"][layer]
                for hf in range(2):
                    def ups(i):
                        for c in range(2):
                            chunk((0, (KC, MC), wsrc(up, 0, KC, i * 2 * MC + (hf * 8 + c) * MC, MC)))
                    loop(sp, vw, 4, {"w": 2}, ups)
                    copy_some(4)

                    def downs(i):
                        for m in range(2):
                            for kk in range(2):
                                chunk((0, (KC, MC), wsrc(down, hf * 16 + kk * KC, KC, i * 2 * MC + m * MC, MC)))
                    loop(sp, vw, 2, {"w": 4}, downs)
                    copy_some(4)

            mlp(0)

            def store_nat(slot, *pairs):
                sp.wait_ge(tile_taken, mark["rows"].pop(0))
                for dst, src in pairs:
                    sp.dma_start(dst, src).then_inc(rows_stored if slot is None else nat_stored[slot], 16)

            ce = GH * E
            stored = [0]

            def store_part(gi, part_):
                wb = min(GROUPS[gi][0], PAST)
                rows = nat[0:NS, stored[0] % 2, :]
                if part_ == 0:
                    store_nat(stored[0] % 2, (io["q_scr"][:, gi * ce:(gi + 1) * ce], rows))
                else:
                    store_nat(stored[0] % 2, (io["ds"][gi][:, wb - 1, (part_ - 1) * ce:part_ * ce], rows))
                stored[0] += 1
                for t in (kept_tiles(gi) if part_ == 1 else []):
                    store_nat(stored[0] % 2, (io["dp"][gi][row0(gi, t):row0(gi, t) + P, 0:ce], nat[:, stored[0] % 2, :]))
                    stored[0] += 1
                for t in (range(NB_T) if part_ == 2 else []):
                    store_nat(None, *([(io["dp"][gi][row0(gi, t):row0(gi, t) + P, ce:2 * ce], dv[:, gi, t, :])]
                                      if t in kept_tiles(gi) else []))

            for p in range(9):
                for c in range(2):
                    chunk((0, (KC, MC), wsrc(io["w_qkv"], 0, KC, p * ce + c * MC, MC)))
                if p:
                    store_part((p - 1) // 3, (p - 1) % 3)
                if p % 3 == 2:
                    copy_some(1)
            for c in range(2):
                chunk((0, (4, 2 * MC), wsrc(io["w_odil"], 0, 4, c * 2 * MC, 2 * MC)))
            store_part(2, 2)
            for n in range(2 * 3 * NS):
                b, gi, which = (n % (3 * NS)) // 3, n % 3, n // (3 * NS)
                w, d = GROUPS[gi]
                if which == 0 and gi == 0:
                    if b == 0:
                        for s_ in range(2):
                            sp.wait_ge(nat_stored[s_], NATS[s_] * 16)
                        sp.wait_ge(output_taken, (H + GH) * NB_T + NS)
                    if due(3 * (b - 1)):
                        sp.wait_ge(cached_used, 3 * (b - 1))
                    sp.dma_start(qb[:, b % 2, :], io["q_scr"][b:b + 1, :].to_broadcast([P, 3 * GH * E])).then_inc(
                        queries_in[b % 2], 16)
                if due(n - 5):
                    sp.wait_ge(cached_used, n - 5)
                wb = min(w, PAST)
                rows = io["state"][gi][b].rearrange("(r s) c -> r s c", s=d)[:, 0, which * GH * E:(which + 1) * GH * E]
                if n == 0:
                    sp.wait_ge(rows_stored, ST_V * 16)
                sp.dma_start(kv[:, n % 6, :], rows).then_inc(cached_in[n % 6], 16)
                if n % 12 == 5:
                    copy_some(1)
            mlp(1)
            copy_some(len(copies))
            sp.wait_ge(tile_taken, mark["last"])
            sp.dma_start(io["yp"].rearrange("(t p) d -> p t d", p=P), yn[:, 0:NB_T, :]).then_inc(rows_stored, 16)
            sp.dma_start(io["ys"], yn[0:NS, NB_T, :]).then_inc(rows_stored, 16)
            sp.wait_ge(latents_stored, 4 * 16)
            sp.wait_ge(states_copied, 16 * len(copies))
            sp.wait_ge(rows_stored, 16 * (2 + ST_V))


        @block.vector
        def _(dve):
            vw = View()

            def link(ins):
                ins.then_inc(dve_step, 1)
                dve.wait_ge(dve_step, vw.tick("dve_step"))

            def z_take(u=None):
                u = vw.n.get("tile_summed", 0) % 4 if u is None else u
                dve.wait_ge(tile_summed, vw.tick("tile_summed"))
                return u

            def free(ins):
                ins.then_inc(tile_taken, 1)

            def zt(u):
                return unit[:, u:u + 1, :, 0:HALF]

            def slot_begin():
                n = vw.tick("a")
                if due(vw.at("a", 4)):
                    dve.wait_ge(tile_low, vw.at("a", 4))
                return (vw.n["a"] - 1) % 4

            def rsqrt(width):
                if due(vw.at("a")):
                    dve.wait_ge(tile_low, vw.at("a"))
                u = z_take()
                x, y = tmp[:, 0, :], tmp[:, 1, :]
                free(dve.tensor_scalar(cols(tmp, 0), zt(u), 1.0 / width, EPS, ALU.mult, ALU.add))
                dve.wait_ge(tile_taken, vw.at("tile_summed"))
                dve.reciprocal(y, x).then_inc(inverse_ready, 1)
                dve.wait_ge(root_ready, vw.tick("root_ready"))
                link(dve.scalar_tensor_tensor(out=y, in0=rstd[:], scalar=-0.5, in1=rstd[:], op0=ALU.mult, op1=ALU.mult))
                link(dve.tensor_tensor(y, y, x, ALU.mult))
                link(dve.scalar_tensor_tensor(out=rstd[:], in0=y, scalar=1.5, in1=rstd[:], op0=ALU.add, op1=ALU.mult))

            def scaled(out, src, g):
                return dve.scalar_tensor_tensor(out=out, in0=src, scalar=gains[:, g:g + 1], in1=rstd[:],
                                                op0=ALU.mult, op1=ALU.mult)

            def norm(g):
                rsqrt(D)
                for f in range(DT):
                    s_ = slot_begin()
                    scaled(tmp[:, s_, :], xT[:, f, :], g + f).then_inc(tile_ready, 1)

            dve.wait_ge(constants_in, 16 * 10)
            for f in range(0, DT, 2):
                u = z_take()
                free(dve.tensor_copy(xT[:, f:f + 2, NS:], ps[:, 2 * u:2 * u + 2, :]))
            u = z_take()
            free(dve.tensor_copy(xT[:, :, 0:NS], ps[:, 2 * u, 0:DT * NS].rearrange("p (f b) -> p f b", f=DT)))
            norm(0)

            for f in range(3):
                u = z_take()
                free(dve.tensor_copy(cols(cq, f), zt(u)))
            for f in range(2):
                u = z_take()
                free(dve.tensor_copy(cols(ckvT, f), zt(u)))

            def rotate(u, out):
                r2 = lambda t: t.rearrange("p (a b) -> p a b", a=2)
                dve.tensor_tensor(r2(rt[64:96, 0, :]), ps[96:128, 2 * u:2 * u + 2, 0:HALF], r2(rope[96:128, :]), ALU.mult)
                link(dve.tensor_tensor(r2(rt[64:96, 1, :]), ps[64:96, 2 * u:2 * u + 2, 0:HALF], r2(rope[64:96, :]), ALU.mult))
                return dve.tensor_tensor(out, rt[64:96, 0, :], rt[64:96, 1, :], ALU.add)

            u = z_take()
            free(rotate(u, kpeT[64:96, :]))
            rsqrt(QL)
            for f in range(3):
                s_ = slot_begin()
                scaled(tmp[:, s_, :], cq[:, f, :], 5 * DT + f).then_inc(tile_ready, 1)
            rsqrt(KVL)
            for f in range(2):
                vw.tick("a")
                scaled(ckvT[:, f, :], ckvT[:, f, :], 5 * DT + 3 + f).then_inc(tile_ready, 1)
            for s_ in range(4):
                dve.tensor_copy(kh[64:96, s_, :], kpeT[64:96, NS:])
            dve.wait_ge(pages_in, 16)
            dve.tensor_copy(ptf[:], pti[:]).then_inc(pages_ready, 1)
            u = z_take()
            free(dve.tensor_copy(ptT[:], ps[0:8, 2 * u, 0:NS * NG]))
            u = z_take()
            free(dve.tensor_scalar(idx[:], ps[:, 2 * u, 0:NS * NG], float(PAGE // KPP), poff[:, 0:1], ALU.mult, ALU.add))
            for t in range(NB_T):
                u = z_take()
                free(dve.tensor_copy(v[:, t, :].rearrange("p (a b) -> p a b", a=2), ps[:, 2 * u:2 * u + 2, :]))
            for t in range(NB_T + 1):
                u = z_take()
                n = NS if t == NB_T else P
                free(dve.tensor_copy(natc[0:n, t, :], ps[0:n, 2 * u, 0:KVL + ROPE]))

            def projected(j, step):
                u = z_take(3)
                if step < 2:
                    h = 2 * j + step
                    dve.tensor_copy(qh[0:NOPE, h % 4, :].rearrange("p (a b) -> p a b", a=2),
                                    ps[0:NOPE, 2 * u:2 * u + 2, 0:HALF])
                    free(rotate(u, qh[64:96, h % 4, :]))
                    dve.wait_ge(tile_taken, vw.at("tile_summed"))
                    link(dve.tensor_copy(qS[:, h, :], qh[:, h % 4, 0:NS]))
                else:
                    dve.tensor_copy(kh[0:NOPE, (2 * j) % 4, :], ps[0:NOPE, 2 * u, :])
                    free(dve.tensor_copy(kh[0:NOPE, (2 * j + 1) % 4, :], ps[NOPE:P, 2 * u, :]))

            for step in range(3):
                projected(0, step)
            for i in range(NI + 1):
                if i < NI:
                    t = i % NB_T
                    dve.wait_ge(scores_ready, i + 1)
                    d = ps[:, i % 2, t * P:(t + 1) * P]
                    link(dve.tensor_tensor(d, d, causal[:], ALU.add))
                    link(dve.tensor_reduce(mxs[:, i % 4:i % 4 + 1], ps[:, i % 2, 0:(t + 1) * P], AX, ALU.max))
                    dve.tensor_scalar(nbs[:, i % 4:i % 4 + 1], mxs[:, i % 4:i % 4 + 1], -MLA_SCALE, None,
                                      ALU.mult).then_inc(max_ready, 1)
                if i % 8 in PROJECT and i < NI - 8:
                    projected(i // 8 + 1, PROJECT.index(i % 8))
                if i >= 1:
                    dve.wait_ge(probs_ready, i)
                    if due(i - 4):
                        dve.wait_ge(output_taken, i - 4)
                    dve.reciprocal(rden[:, (i - 1) % 4:(i - 1) % 4 + 1], den[:, (i - 1) % 4:(i - 1) % 4 + 1]).then_inc(reciprocal_ready, 1)
            for f in range(DT):
                s_ = slot_begin()
                u = z_take()
                free(dve.tensor_copy(tmp[:, s_, NS:], ps[:, 2 * u, :]))
            for q4 in range(4):
                u = z_take()
                free(dve.tensor_copy(wukT[:, 4 * q4:4 * q4 + 4, :].rearrange("p h c -> p (h c)").rearrange(
                    "p (a b) -> p a b", a=2), ps[0:NOPE, 2 * u:2 * u + 2, :]))
            u = z_take()
            dve.tensor_copy(qlat[:, :, 0, :], ps[:, 2 * u, 0:P].rearrange("p (h b) -> p b h", h=H))
            free(dve.tensor_copy(qlat[:, :, 1, :], ps[:, 2 * u + 1, 0:P].rearrange("p (h b) -> p b h", h=H)))
            link(dve.memset(bd[:], 0.0))
            for s_ in range(4):
                ins = dve.tensor_copy(bd[32 * s_:32 * s_ + 32, :, s_, :], qS[64:96, :, :].rearrange("p h b -> p b h"))
            ins.then_inc(rotary_ready, 1)

            def keys_out(m):
                if due(m - 1):
                    dve.wait_ge(keys_used, m - 1)
                for hf in range(2):
                    dve.wait_ge(keys_turned, 3 * m + hf + 1)
                    dve.tensor_copy(cT[:, m % 2, 2 * hf:2 * hf + 2, :, :].rearrange("p s k c -> p (s k c)"),
                                    ps[:, hf, :]).then_inc(keys_taken, 1)
                dve.wait_ge(keys_turned, 3 * m + 3)
                dve.tensor_copy(kT4[:, m % 2, :], ps[:, 2, 0:P]).then_inc(keys_taken, 1)

            def part_max(b):
                dve.wait_ge(scores_ready, NI + b + 1)
                link(dve.tensor_reduce(mb[:, 0, :], ps[:, 4 + b % 2, :].rearrange("p (c h) -> p h c", h=H), AX, ALU.max))
                dve.tensor_tensor(mb[:, 0, :], mb[:, 0, :], ps[:, 6, 0:H], ALU.max).then_inc(max_ready, 1)

            def full_max(b):
                dve.wait_ge(max_spread, 2 * b + 1)
                link(dve.tensor_reduce(mxs[0:H, 0:1], ps[0:H, 3, 0:P], AX, ALU.max))
                dve.tensor_scalar(sm[0:H, :], ident[0:H, 0:H], mxs[0:H, 0:1], None, ALU.mult).then_inc(max_ready, 1)
                dve.wait_ge(max_spread, 2 * b + 2)
                link(dve.tensor_copy(mb[:, 1, :], ps[:, 3, P:P + H]))
                dve.wait_ge(output_ready, NI + b)
                m_all = mb[:, 1, :].rearrange("p (o h) -> p o h", o=1)
                dve.tensor_tensor(psm[:, 0:32 * H].rearrange("p (c h) -> p c h", h=H),
                                  ps[:, 4 + b % 2, :].rearrange("p (c h) -> p c h", h=H),
                                  m_all.to_broadcast([P, 32, H]), ALU.subtract)
                dve.tensor_tensor(psm[:, 32 * H:], ps[:, 6, 0:H], mb[:, 1, :], ALU.subtract).then_inc(exponents_ready, 1)

            def part_sum(b):
                dve.wait_ge(probs_ready, NI + b + 1)
                dve.tensor_reduce(mb[:, 1, :], psm[:, 0:32 * H].rearrange("p (c h) -> p h c", h=H), AX,
                                  ALU.add).then_inc(max_ready, 1)

            def latent_out(b):
                dve.wait_ge(output_ready, NI + b + 1)
                link(dve.tensor_tensor(mb[:, 0, :], ps[:, 7, 2 * H:3 * H], psm[:, 32 * H:], ALU.add))
                link(dve.reciprocal(mb[:, 0, :], mb[:, 0, :]))
                for k in range(2):
                    link(dve.scalar_tensor_tensor(out=sm[:], in0=psm[:, 32 * H:], scalar=ckvT[:, k, b:b + 1],
                                                  in1=ps[:, 7, k * H:(k + 1) * H], op0=ALU.mult, op1=ALU.add))
                    ins = dve.tensor_tensor(olat[:, k, :, b], sm[:], mb[:, 0, :], ALU.mult)
                    if k == 0:
                        link(ins)
                ins.then_inc(output_taken, 1)

            keys_out(0)
            for b in range(NS):
                for q8 in range(8):
                    m = b * 8 + q8
                    if m + 1 < NS * 8:
                        keys_out(m + 1)
                    if b and q8 == 0:
                        part_max(b - 1)
                    if b and q8 == 1:
                        full_max(b - 1)
                    if b and q8 == 2:
                        part_sum(b - 1)
                    if b and q8 == 3:
                        latent_out(b - 1)
            part_max(NS - 1)
            full_max(NS - 1)
            part_sum(NS - 1)
            latent_out(NS - 1)
            u = z_take()
            vw.tick("a")
            free(dve.tensor_copy(oS[:], ps[:, 2 * u, 0:DT * NS].rearrange("p (f b) -> p f b", f=DT)))

            def residual(f):
                u = z_take()
                free(dve.tensor_tensor(cols(xT, f), cols(xT, f), zt(u), ALU.add))

            for f in range(DT):
                residual(f)

            def mlp(g):
                norm(g)
                for hf in range(2):
                    def up(i):
                        for j in range(4):
                            u = z_take()
                            s_ = slot_begin()
                            out = cols(tmp, s_)
                            free(dve.tensor_scalar(out, zt(u), 0.0, None, ALU.max))
                            dve.wait_ge(tile_taken, vw.at("tile_summed"))
                            dve.tensor_tensor(tmp[:, s_, :], tmp[:, s_, :], tmp[:, s_, :], ALU.mult).then_inc(tile_ready, 1)
                    loop(dve, vw, 4, {"tile_summed": 4, "a": 4}, up)
                    loop(dve, vw, 2, {"tile_summed": 4}, lambda i: [residual(i * 4 + j) for j in range(4)])

            mlp(DT)

            norm(2 * DT)
            nn = 0

            def row_tile(n, out):
                u = z_take()
                free(dve.tensor_copy(out, ps[0:n, 2 * u, :]))

            dve.wait_ge(tile_low, vw.at("a"))
            for gi in range(3):
                for part_ in range(3):
                    for f in range(4):
                        u = z_take()
                        out = cols(tmp, f) if part_ == 2 else (dq, dk)[part_][:, gi, f:f + 1, :].rearrange(
                            "p f (a b) -> p f a b", a=2)
                        free(dve.tensor_copy(out, zt(u)))
                        if part_ == 2:
                            dve.wait_ge(tile_taken, vw.at("tile_summed"))
                            dve.tensor_copy(vS[:, gi, f, :], tmp[:, f, 0:NS])
                    if due(16 * (nn // 2)):
                        dve.wait_ge(nat_stored[nn % 2], 16 * (nn // 2))
                    row_tile(NS, nat[0:NS, nn % 2, :])
                    nn += 1
                    for t in (kept_tiles(gi) if part_ == 1 else []):
                        dve.wait_ge(nat_stored[nn % 2], 16 * (nn // 2))
                        row_tile(P, nat[:, nn % 2, :])
                        nn += 1
                    for t in (range(NB_T) if part_ == 2 else []):
                        row_tile(P, dv[:, gi, t, :])
            dve.tensor_tensor(prodS[:], dq[:, :, :, 0:NS], dk[:, :, :, 0:NS], ALU.mult).then_inc(products_ready, 1)
            u = z_take()
            for hp in range(2):
                ins = dve.tensor_copy(sN[:, :, hp::2, :], ps[:, 2 * u, hp * 96:(hp + 1) * 96].rearrange(
                    "p (g t b) -> p g t b", g=3, t=4))
            free(ins)

            DI = GH * NB_T
            turned = [0]

            def d_max(i):
                h, t = i // NB_T, i % NB_T
                if i >= 2:
                    turned[0] += n_parts((i - 2) % NB_T)
                dve.wait_ge(scores_ready, NI + NS + i + 1)
                dve.wait_ge(turned_ready, NI + turned[0])
                base, at_ = 3 * (i % 2), 0
                for g in range(3):
                    if g == 0:
                        c0, c1 = (P if t == 0 else 0), 2 * P
                    else:
                        c1 = 2 * P + g * 4 * P
                        c0 = c1 - (t + 1) * P
                    w = c1 - c0
                    ins = dve.scalar_tensor_tensor(out=sc[:, i % 2, at_:at_ + w], in0=dist[:, c0:c1],
                                                   scalar=-(2.0 ** -(h + 1)) / DIL_SCALE, in1=ps[:, base + g, 0:w],
                                                   op0=ALU.mult, op1=ALU.add)
                    at_ += w
                ins.then_inc(dil_scores_taken, 1)
                dve.wait_ge(dil_scores_taken, i + 1)
                link(dve.tensor_reduce(mxs[:, i % 4:i % 4 + 1], sc[:, i % 2, 0:at_], AX, ALU.max))
                dve.tensor_scalar(nbs[:, i % 4:i % 4 + 1], mxs[:, i % 4:i % 4 + 1], -DIL_SCALE, None,
                                  ALU.mult).then_inc(max_ready, 1)

            d_max(0)
            for i in range(DI):
                if i + 1 < DI:
                    d_max(i + 1)
                dve.wait_ge(probs_ready, NI + NS + i + 1)
                dve.wait_ge(output_taken, NI + NS + i - 3)
                dve.reciprocal(rden[:, i % 4:i % 4 + 1], den[:, i % 4:i % 4 + 1]).then_inc(reciprocal_ready, 1)

            for n in range(3 * NS):
                b, gi = n // 3, n % 3
                dve.wait_ge(queries_in[b % 2], 16 * (b // 2 + 1))
                dve.wait_ge(cached_in[n % 6], 16 * (n // 6 + 1))
                dve.tensor_tensor(pv_[:, n % 2, :], kv[:, n % 6, :], qb[:, b % 2, gi * GH * E:(gi + 1) * GH * E],
                                  ALU.mult).then_inc(cached_used, 1)
                dve.wait_ge(cached_used, n + 1)
                link(dve.tensor_reduce(sS[:, gi, b, :], pv_[:, n % 2, :].rearrange("p (h e) -> p h e", h=GH), AX, ALU.add))
            bh = lambda t: t.rearrange("p (b h) -> p b h", b=NS)
            for g in range(3):
                ins = dve.tensor_tensor(sS[:, g, :, :], sS[:, g, :, :],
                                        sdist[:, g * GH:(g + 1) * GH].rearrange("p (o h) -> p o h", o=1).to_broadcast([P, NS, GH]),
                                        ALU.add)
            link(ins)
            m0 = bh(mS[:, 0, :])
            new = lambda g: sN[:, g, :, :].rearrange("p h b -> p b h")
            link(dve.tensor_tensor(m0, sS[:, 0, :, :], sS[:, 1, :, :], ALU.max))
            link(dve.tensor_tensor(m0, m0, sS[:, 2, :, :], ALU.max))
            link(dve.tensor_tensor(m0, m0, new(0), ALU.max))
            link(dve.tensor_tensor(m0, m0, new(1), ALU.max))
            dve.tensor_tensor(m0, m0, new(2), ALU.max).then_inc(max_ready, 1)
            dve.wait_ge(max_spread, 2 * NS + 1)
            link(dve.tensor_reduce(mxs[0:64, 0:1], ps[0:64, 0, 0:P], AX, ALU.max))
            dve.tensor_scalar(mS[0:64, 1, :], ident[0:64, 0:64], mxs[0:64, 0:1], None, ALU.mult).then_inc(max_ready, 1)
            dve.wait_ge(max_spread, 2 * NS + 2)
            link(dve.tensor_copy(mS[:, 2, :], ps[:, 1, 0:64]))
            for g in range(3):
                dve.tensor_tensor(sS[:, g, :, :], sS[:, g, :, :], bh(mS[:, 2, :]), ALU.subtract)
                ins = dve.tensor_tensor(new(g), new(g), bh(mS[:, 2, :]), ALU.subtract)
            ins.then_inc(exponents_ready, 1)
            dve.wait_ge(probs_ready, NI + NS + DI + 1)
            m3 = bh(mS[:, 3, :])
            link(dve.tensor_tensor(m3, sS[:, 0, :, :], sS[:, 1, :, :], ALU.add))
            dve.tensor_tensor(m3, m3, sS[:, 2, :, :], ALU.add).then_inc(max_ready, 1)
            dve.wait_ge(max_spread, 2 * NS + 3)
            m2 = bh(mS[:, 2, :])
            link(dve.tensor_tensor(m2, new(0), bh(ps[:, 2, 0:64]), ALU.add))
            link(dve.tensor_tensor(m2, m2, new(1), ALU.add))
            link(dve.tensor_tensor(m2, m2, new(2), ALU.add))
            link(dve.reciprocal(mS[:, 2, :], mS[:, 2, :]))
            dve.wait_ge(cached_used, 6 * NS)
            for hp in range(2):
                r = slice(hp * E, (hp + 1) * E)
                link(dve.tensor_tensor(prodS[r], vS[r], sN[r, :, hp::2, :], ALU.mult))
                link(dve.tensor_tensor(prodS[r, 0], prodS[r, 0], prodS[r, 1], ALU.add))
                link(dve.tensor_tensor(prodS[r, 0], prodS[r, 0], prodS[r, 2], ALU.add))
                mine = ps[r, 4, 0:256].rearrange("p (b x) -> p x b", b=NS)[:, hp::10, :]
                link(dve.tensor_tensor(prodS[r, 0], prodS[r, 0], mine, ALU.add))
                rd = mS[r, 2, :].rearrange("p (b h) -> p h b", b=NS)[:, hp::2, :]
                ins = dve.tensor_tensor(oSd[r], prodS[r, 0], rd, ALU.mult)
                if hp == 0:
                    link(ins)
            ins.then_inc(output_taken, 1)
            dve.wait_ge(output_taken, NI + NS + DI + 1)
            for f in range(4):
                s_ = slot_begin()
                u = z_take()
                dve.tensor_copy(tmp[:, s_, 0:NS], oSd[:, f, :])
                free(dve.tensor_copy(tmp[:, s_, NS:], ps[:, 2 * u, :]))
            for f in range(DT):
                residual(f)
            mlp(3 * DT)
            rsqrt(D)
            dve.wait_ge(tile_low, vw.at("a"))

            def final(f):
                scaled(tmp[:, f % 4, :], xT[:, f, :], 4 * DT + f).then_inc(final_ready, 1)

            final(0)
            for f in range(DT):
                if f + 1 < DT:
                    final(f + 1)
                u = z_take()
                c = slice(f * P, (f + 1) * P)
                dve.tensor_copy(yn[:, 0:NB_T, c], ps[:, 2 * u, :].rearrange("p (t c) -> p t c", t=NB_T))
                free(dve.tensor_copy(yn[0:NS, NB_T, c], ps[0:NS, 2 * u + 1, 0:P]))

        @block.scalar
        def _(act):
            vw = View()
            landed = [0, 0]

            def split_w(z=True):
                c = vw.n.get("w", 0)
                kind = KINDS[c] if vw.i is None and c < len(KINDS) else full
                if z:
                    act.wait_ge(tile_summed, vw.at("tile_summed"))
                slot = c % 2
                vw.tick("w")
                vw.tick(f"chunk_in{slot}", PIECES[kind])
                n = vw.at(f"chunk_in{slot}")
                act.wait_ge(chunk_in[slot], n * 16)
                for dst, src in kind(slot):
                    ins = act.activation(dst(0), src, ACT.Copy)
                ins.then_inc(chunk_high, 1)

            def split(dst, src, z=False):
                n = vw.tick("a")
                if z:
                    act.wait_ge(tile_taken, vw.tick("tile_summed"))
                else:
                    act.wait_ge(tile_ready, vw.tick("tile_ready"))
                act.activation(dst, src, ACT.Copy).then_inc(tile_high, 1)

            def slot():
                return vw.n.get("a", 0) % 4

            def root():
                act.wait_ge(inverse_ready, vw.tick("inverse_ready"))
                act.activation(rstd[:], tmp[:, 1, :], ACT.Sqrt).then_inc(root_ready, 1)

            def squares(src, nt, zs):
                for f in range(nt):
                    n = vw.tick("squares_ready")
                    act.wait_ge(tile_taken, zs - nt + 1 + f if nt == DT and zs > 8 else zs)
                    if due(n - 2 - vw.n.get("norms", 0)):
                        act.wait_ge(squares_used, n - 2 - vw.n.get("norms", 0))
                    if vw.n.get("norms", 0) and f < 2:
                        act.wait_ge(tile_summed, vw.at("tile_summed"))
                    act.activation(sq[:, (n - 1) % 2, :], src(f), ACT.Square).then_inc(squares_ready, 1)
                vw.tick("norms")
                vw.tick("tile_summed")

            act.wait_ge(constants_in, 16 * 10)
            split_w(z=False)
            split_w(z=False)
            vw.tick("tile_summed", 5)
            xsrc = lambda f: xT[:, f, :]

            def norm():
                squares(xsrc, DT, vw.at("tile_summed"))
                root()
                for f in range(DT):
                    split(hA[:, f, 0, :], tmp[:, slot(), :])

            norm()
            for n in (2, 1, 2, 1):
                vw.tick("tile_summed", n)
                split_w()
            squares(lambda f: cq[:, f, :], 3, vw.at("tile_summed"))
            squares(lambda f: ckvT[:, f, :], 2, vw.at("tile_summed") - 1)
            root()
            for f in range(3):
                split(hA[:, f, 0, :], tmp[:, slot(), :])
            root()
            for f in range(2):
                split(ckvH[:, f, 0, :], ckvT[:, f, :])
            vw.tick("tile_summed", 2 + NB_T)
            split_w()
            vw.tick("tile_summed", NB_T + 1)
            vw.tick("tile_summed", 3)
            split_w()
            act.wait_ge(latents_stored, 4 * 16)
            for i in range(NI + 2):
                if i < NI:
                    t = i % NB_T
                    act.wait_ge(max_ready, i + 1)
                    if due(i - 1):
                        act.wait_ge(turned_ready, i - 1)
                    if due(i - 3):
                        act.wait_ge(reciprocal_ready, i - 3)
                    act.activation(pr[:, i % 2, 0:(t + 1) * P], ps[:, i % 2, 0:(t + 1) * P], ACT.Exp,
                                   bias=nbs[:, i % 4:i % 4 + 1], scale=MLA_SCALE,
                                   accum_out=den[:, i % 4:i % 4 + 1]).then_inc(probs_ready, 1)
                if 1 <= i <= NI:
                    j = i - 1
                    act.wait_ge(turned_ready, j + 1)
                    if due(j - 1):
                        act.wait_ge(output_ready, j - 1)
                    w = (j % NB_T + 1) * P
                    act.activation(pT[:, j % 2, 0:w], ps[:, 2 + j % 2, 0:w], ACT.Copy).then_inc(turned_taken, 1)
                if i >= 2:
                    j = i - 2
                    h, t = j // NB_T, j % NB_T
                    act.wait_ge(output_ready, j + 1)
                    act.wait_ge(reciprocal_ready, j + 1)
                    act.activation(onat[:, t, h * VD:(h + 1) * VD], ps[:, 4 + j % 2, 0:VD], ACT.Copy,
                                   scale=rden[:, j % 4:j % 4 + 1]).then_inc(output_taken, 1)
                if i % 8 == 7 and i < NI - 8:
                    vw.tick("tile_summed", 3)
                    split_w()
            for f in range(DT):
                split(hA[:, f, 0, NS:], tmp[:, slot(), NS:], z=True)
            vw.tick("tile_summed", 5)
            for b in range(NS):
                act.wait_ge(exponents_ready, b + 1)
                act.activation(psm[:], psm[:], ACT.Exp, scale=MLA_SCALE).then_inc(probs_ready, 1)
            split(hA[:, :, 0, 0:NS], oS[:], z=True)
            for c in range(4):
                vw.tick("tile_summed", 2)
                split_w()

            def mlp(last=False):
                norm()
                for hf in range(2):
                    def up(i):
                        for c in range(2):
                            for j in range(2):
                                split(part(uT, i * 4 + 2 * c + j, 0), tmp[:, slot():slot() + 1, :])
                                vw.tick("tile_summed")
                            split_w()
                    loop(act, vw, 4, {"w": 2, "chunk_in0": 1, "chunk_in1": 1, "tile_summed": 4, "a": 4, "tile_ready": 4}, up)

                    def down(i):
                        for m in range(2):
                            act.wait_ge(first_chunk_used, vw.tick("first_chunk_used"))
                            split_w(z=False)
                            vw.tick("tile_summed", 2)
                            split_w()
                    if last and hf:
                        down(0)
                        act.wait_ge(first_chunk_used, vw.tick("first_chunk_used"))
                        split_w(z=False)
                        vw.tick("tile_summed", 2)
                        split_w()
                        vw.tick("tile_summed", 2)
                    else:
                        loop(act, vw, 2, {"w": 4, "chunk_in0": 2, "chunk_in1": 2, "tile_summed": 4, "first_chunk_used": 2}, down)

            mlp()
            norm()
            for gi in range(3):
                for part_ in range(3):
                    for c in range(2):
                        vw.tick("tile_summed", 2)
                        split_w()
                    vw.tick("tile_summed", 1 + (len(kept_tiles(gi)) if part_ == 1 else NB_T if part_ == 2 else 0))
            vw.tick("tile_summed")
            DI = GH * NB_T
            done = [0, 0]

            def d_exp(i):
                w = (min(i % NB_T + 1, 2) + 2 * (i % NB_T + 1)) * P
                act.wait_ge(max_ready, NI + 3 * NS + i + 1)
                act.wait_ge(reciprocal_ready, NI + i - 3)
                act.activation(sc[:, i % 2, 0:w], sc[:, i % 2, 0:w], ACT.Exp, bias=nbs[:, i % 4:i % 4 + 1],
                               scale=DIL_SCALE, accum_out=den[:, i % 4:i % 4 + 1]).then_inc(probs_ready, 1)

            d_exp(0)
            for i in range(DI):
                h, t = i // NB_T, i % NB_T
                if i + 1 < DI:
                    d_exp(i + 1)
                n_blocks = min(t + 1, 2) + 2 * (t + 1)
                for k in range(n_parts(t)):
                    n = done[0]
                    w = min(4, n_blocks - 4 * k) * P
                    act.wait_ge(turned_ready, NI + n + 1)
                    if due(n - 3):
                        act.wait_ge(values_used, n - 3)
                    act.activation(scT[:, n % 4, 0:w], ps[:, 6 + n % 2, 0:w], ACT.Copy).then_inc(turned_taken, 1)
                    done[0] += 1
                act.wait_ge(values_used, done[0])
                act.wait_ge(reciprocal_ready, NI + i + 1)
                act.activation(ond[:, t, h * E:(h + 1) * E], ps[:, 3 * (i % 2), 2 * P:2 * P + E], ACT.Copy,
                               scale=rden[:, i % 4:i % 4 + 1]).then_inc(output_taken, 1)
            act.wait_ge(exponents_ready, NS + 1)
            act.activation(sS[:], sS[:], ACT.Exp, scale=DIL_SCALE)
            act.activation(sN[:], sN[:], ACT.Exp, scale=DIL_SCALE).then_inc(probs_ready, 1)
            for f in range(4):
                split(hA[:, f, 0, :], tmp[:, slot(), :], z=True)
            for c in range(2):
                vw.tick("tile_summed", 4)
                split_w()
            mlp(last=True)
            squares(xsrc, DT, vw.at("tile_summed"))
            root()

        @block.gpsimd
        def _(pool):
            vw = View()

            def sub(dst, src, hi):
                return pool.tensor_tensor(dst, src, hi.bitcast(F32), ALU.subtract)

            def split_w():
                c = vw.n.get("w", 0)
                kind = KINDS[c] if vw.i is None and c < len(KINDS) else full
                pool.wait_ge(chunk_high, vw.tick("w"))
                for dst, src in kind(c % 2):
                    ins = sub(dst(1), src, dst(0))
                ins.then_inc(chunk_low, 1)

            def split(dst, src, hi):
                pool.wait_ge(tile_high, vw.tick("a"))
                sub(dst, src, hi).then_inc(tile_low, 1)

            def slot():
                return vw.n.get("a", 0) % 4

            def h_tile(f, c=slice(0, T)):
                split(hA[:, f, 1, c], tmp[:, slot(), c], hA[:, f, 0, c])

            split_w()
            split_w()
            for f in range(DT):
                h_tile(f)
            for n in range(4):
                split_w()
            for f in range(3):
                h_tile(f)
            for f in range(2):
                split(ckvH[:, f, 1, :], ckvT[:, f, :], ckvH[:, f, 0, :])
            for n in range(1 + H // 2):
                split_w()
            for f in range(DT):
                h_tile(f, slice(NS, T))
            pool.wait_ge(tile_taken, mark["qlat"])
            for g in range(NS * NG):
                if due(g - GR + 1):
                    pool.wait_ge(gather_used, g - GR + 1)
                where = bass.IndirectOffsetOnAxis(ap=idx[:, g:g + 1], axis=0)
                pool.indirect_dma_start(gat[:, g % GR, :], None, io["ckv_pool"], where).then_inc(gather_in[g % GR], 16)
                pool.indirect_dma_start(gkp[:, g % GR, :], None, io["kpe_pool"], where).then_inc(gather_in[g % GR], 16)
            split(hA[:, :, 1, 0:NS], oS[:], hA[:, :, 0, 0:NS])
            for n in range(4):
                split_w()

            def mlp(last=False):
                for f in range(DT):
                    h_tile(f)
                for hf in range(2):
                    def up(i):
                        for c in range(2):
                            for j in range(2):
                                f = i * 4 + 2 * c + j
                                split(part(uT, f, 1), tmp[:, slot():slot() + 1, :], part(uT, f, 0))
                            split_w()
                    loop(pool, vw, 4, {"w": 2, "a": 4}, up)
                    if last and hf:
                        for n in range(6):
                            split_w()
                    else:
                        loop(pool, vw, 2, {"w": 4}, lambda i: [split_w() for _ in range(4)])

            mlp()
            for f in range(DT):
                h_tile(f)
            for n in range(18):
                split_w()
            for f in range(4):
                h_tile(f)
            for n in range(2):
                split_w()
            mlp(last=True)


def constants():
    half = ROPE // 2
    inv = np.float32(10000.0) ** (-np.arange(half, dtype=np.float32) / np.float32(half))
    pos = np.concatenate([np.full(NS, PAST), np.arange(NP)]).astype(np.float32)
    ang = (pos[:, None] * inv[None, :].astype(np.float32)).astype(np.float32).T
    rope = np.zeros((P, T), np.float32)
    rope[64:96] = np.concatenate([np.cos(ang), np.cos(ang)])
    rope[96:128] = np.concatenate([-np.sin(ang), np.sin(ang)])
    i = np.arange(P)
    causal = np.where(i[None, :] <= i[:, None], 0.0, 10 * NEG).astype(np.float32)
    far = -NEG * 256
    blocks = []
    for w, d in GROUPS:
        for off in ((1, 0) if d == 1 else (3, 2, 1, 0)):
            dd = off * P + i[:, None] - i[None, :]
            ok = (dd >= 0) & (dd % d == 0) & (dd <= w)
            blocks.append(np.where(ok, dd, far))
    slopes = 2.0 ** -(np.arange(1, GH + 1))
    sd = np.concatenate([-(d * (P - i))[:, None] * slopes[None, :] / DIL_SCALE for _, d in GROUPS], 1)
    halves = np.zeros((P, 2, P), np.float32)
    halves[0:64, 0], halves[64:, 1] = 1, 1
    return {
        "ident": np.eye(P, dtype=np.float32), "ones": np.ones((P, P), np.float32), "rope": rope, "causal": causal,
        "dist": np.concatenate(blocks, 1).astype(np.float32), "sdist": sd.astype(np.float32),
        "half": halves.reshape(P, 2 * P),
        "sel": (i[None, :] // 16 == np.arange(8)[:, None]).astype(np.float32),
        "poff": (i % 16).astype(np.float32)[:, None],
    }


def kernel(**inputs):
    import concourse.bacc as bacc
    from concourse.bass_utils import run_bass_kernel_spmd

    a = {k: np.asarray(x) for k, x in inputs.items()}
    columns = lambda x: x.reshape(-1, P).T
    arrays = {
        "xp": a["x_prompt"].reshape(NP, D), "xs": a["x_sample"].reshape(NS, D),
        "ckv_pool": a["cache_mla_ckv"].reshape(-1, KPP * KVL), "kpe_pool": a["cache_mla_kpe"].reshape(-1, KPP * ROPE),
        "pt": a["page_table"].reshape(NS * NG, 8),
        "state0": a["state_dil_kv_w128"].reshape(NS, -1, 2 * GH * E),
        "state1": a["state_dil_kv_w512"].reshape(NS, -1, 2 * GH * E),
        "state2": a["state_dil_kv_w2048"].reshape(NS, -1, 2 * GH * E),
        "w_dq": a["mla_w_dq"][0], "w_uq": a["mla_w_uq"][0], "w_dkv": a["mla_w_dkv"][0],
        "w_uk": a["mla_w_uk"].reshape(KVL, H * NOPE), "w_uv": a["mla_w_uv"].reshape(KVL, H * VD),
        "w_omla": a["mla_w_o"][0], "w_qkv": a["dil_w_qkv"][0], "w_odil": a["dil_w_o"][0],
        "w_up": a["ffn_w_up"], "w_down": a["ffn_w_down"],
        "gains": np.concatenate([columns(x) for x in (
            a["norm_mix"][0], a["norm_ffn"][0], a["norm_mix"][1], a["norm_ffn"][1], a["norm_final"],
            a["mla_g_q"][0], a["mla_g_kv"][0])], 1),
    } | constants()
    outs = {"yp": (NP, D), "ys": (NS, D), "ckv_p": (NP, KVL), "kpe_p": (NP, ROPE), "ckv_s": (NS, KVL), "kpe_s": (NS, ROPE)}
    for gi, (w, d) in enumerate(GROUPS):
        outs[f"dp{gi}"] = (min(w, NP), 2 * GH * E)
        outs[f"ds{gi}"] = (NS, min(w, PAST + 1), 2 * GH * E)
    nc = bacc.Bacc("TRN2", target_bir_lowering=False, num_devices=1)
    io, feed = {}, {}
    for name, x in arrays.items():
        x = np.ascontiguousarray(x)
        feed[f"in_{name}"] = x
        io[name] = nc.dram_tensor(f"in_{name}", x.shape, mybir.dt.from_np(x.dtype), kind="ExternalInput").ap()
    for name, shape in outs.items():
        io[name] = nc.dram_tensor(f"out_{name}", shape, F32, kind="ExternalOutput").ap()
    io["q_scr"] = nc.dram_tensor("q_scratch", (NS, 3 * GH * E), F32, kind="Internal").ap()
    io["state"] = [io[f"state{g}"] for g in range(3)]
    io["dp"] = [io[f"dp{g}"] for g in range(3)]
    io["ds"] = [io[f"ds{g}"] for g in range(3)]
    program(nc, io)
    got = run_bass_kernel_spmd(nc, [feed], core_ids=[0]).results[0]
    r = lambda name, *shape: got[f"out_{name}"].reshape(shape)
    return (
        r("yp", 1, NP, D), r("ys", NS, 1, D), r("ckv_p", 1, 1, NP, KVL), r("kpe_p", 1, 1, NP, ROPE),
        r("ckv_s", 1, NS, 1, KVL), r("kpe_s", 1, NS, 1, ROPE),
        *[r(f"dp{g}", 1, 1, min(w, NP), 2, GH, E) for g, (w, d) in enumerate(GROUPS)],
        *[r(f"ds{g}", 1, NS, min(w, PAST + 1), 2, GH, E) for g, (w, d) in enumerate(GROUPS)],
    )
```
